# Optimizing a Trainium2 kernel written in Bass

```python
import math
import jax, jax.numpy as jnp
from jax import lax
import numpy as np

D_MODEL = 1024
BATCH = 1
SEQ = 1024
DEPTH = 2

HEAD_DIM = 64
GRID_W = 64
RMS_EPS = 1e-6
NEG = -1e30

A_HEADS = 8
B_HEADS = 8
DILATED_BRANCHES = ((128, 1), (512, 4), (2048, 16))
WIN_BLOCK = 128
NA_ROWS = 8
NA_COLS = 16

C_HEADS = 16
Q_LORA = 384
KV_LORA = 128
QK_NOPE = 64
QK_ROPE = 32
V_DIM = 64
ROPE_THETA = 10000.0
Q_BLOCK = 128

T5_BUCKETS = 32
T5_MAX_DIST = 1024
T5_HEADS = max(A_HEADS, C_HEADS)

D_FF = -(-8 * D_MODEL // (3 * 256)) * 256

N_EVEN = (DEPTH + 1) // 2
N_ODD = DEPTH // 2

kernel_name = "hybrid_dilated_natten_mla_encoder"

def rmsnorm(x, g):
    xf = x.astype(jnp.float32)
    y = xf * lax.rsqrt(jnp.mean(xf * xf, axis=-1, keepdims=True) + RMS_EPS)
    return (y * g.astype(jnp.float32)).astype(x.dtype)

def t5_bucket(rel):
    half = T5_BUCKETS // 2
    max_exact = half // 2
    n = jnp.abs(rel)
    nf = jnp.maximum(n, max_exact).astype(jnp.float32)
    large = max_exact + (jnp.log(nf / max_exact) / math.log(T5_MAX_DIST / max_exact)
                         * (half - max_exact)).astype(jnp.int32)
    large = jnp.minimum(large, half - 1)
    return jnp.where(rel > 0, half, 0) + jnp.where(n < max_exact, n, large)

def t5_bias(t5_table, rel, n_heads):
    return t5_table[:, :n_heads].T[:, t5_bucket(rel)].astype(jnp.float32)

def dilated_branch(q, k, v, t5_table, window, dil):
    B, S, H, D = q.shape
    side = window // (2 * dil)
    L = S // dil
    nb = -(-L // WIN_BLOCK)
    Lp = nb * WIN_BLOCK
    span = WIN_BLOCK + 2 * side

    def to_sub(a):
        return a.reshape(B, L, dil, H, D).transpose(0, 2, 1, 3, 4)

    qs = jnp.pad(to_sub(q), ((0, 0), (0, 0), (0, Lp - L), (0, 0), (0, 0)))
    qs = qs.reshape(B, dil, nb, WIN_BLOCK, H, D)
    kv_pad = ((0, 0), (0, 0), (side, Lp - L + side), (0, 0), (0, 0))
    ks = jnp.pad(to_sub(k), kv_pad)
    vs = jnp.pad(to_sub(v), kv_pad)
    idx = jnp.arange(nb)[:, None] * WIN_BLOCK + jnp.arange(span)[None, :]
    kb = ks[:, :, idx]
    vb = vs[:, :, idx]

    s = jnp.einsum('brnqhd,brnkhd->brnhqk', qs, kb).astype(jnp.float32) * (D ** -0.5)
    j = jnp.arange(span)[None, :] - side - jnp.arange(WIN_BLOCK)[:, None]
    mk = idx - side
    valid = (jnp.abs(j) <= side)[None] & ((mk >= 0) & (mk < L))[:, None, :]
    s = s + t5_bias(t5_table, j * dil, H)[None, None, None]
    s = jnp.where(valid[None, None, :, None], s, NEG)
    m = jnp.max(s, axis=-1, keepdims=True)
    p = jnp.exp(s - m)
    den = jnp.sum(p, axis=-1, keepdims=True)
    o = jnp.einsum('brnhqk,brnkhd->brnqhd', (p / den).astype(v.dtype), vb)
    lse = (m + jnp.log(den))[..., 0]

    o = o.reshape(B, dil, Lp, H, D)[:, :, :L].transpose(0, 2, 1, 3, 4).reshape(B, S, H, D)
    lse = lse.transpose(0, 1, 2, 4, 3).reshape(B, dil, Lp, H)[:, :, :L]
    lse = lse.transpose(0, 2, 1, 3).reshape(B, S, H)
    return o, lse

def dilated_mixture(q, k, v, t5_table):
    outs, lses = [], []
    for window, dil in DILATED_BRANCHES:
        o, l = dilated_branch(q, k, v, t5_table, window, dil)
        outs.append(o)
        lses.append(l)
    w = jax.nn.softmax(jnp.stack(lses, axis=0), axis=0)
    o = jnp.sum(w[..., None] * jnp.stack(outs, axis=0).astype(jnp.float32), axis=0)
    return o.astype(q.dtype)

def neighbourhood_attention(q, k, v, rpb):
    B, S, H, D = q.shape
    rows = S // GRID_W
    kr = min(NA_ROWS, rows)
    kc = NA_COLS
    qg = q.reshape(B, rows, GRID_W, H, D)
    kg = k.reshape(B, rows, GRID_W, H, D)
    vg = v.reshape(B, rows, GRID_W, H, D)
    r = jnp.arange(rows)
    r0 = jnp.clip(r - kr // 2, 0, rows - kr)
    row_idx = r0[:, None] + jnp.arange(kr)[None, :]
    kb = kg[:, row_idx]
    vb = vg[:, row_idx]
    c = jnp.arange(GRID_W)
    c0 = jnp.clip(c - kc // 2, 0, GRID_W - kc)
    col_ok = (c[None, :] >= c0[:, None]) & (c[None, :] < c0[:, None] + kc)

    s = jnp.einsum('brqhd,brkwhd->bhrqkw', qg, kb).astype(jnp.float32) * (D ** -0.5)
    roff = row_idx - r[:, None] + (NA_ROWS - 1)
    coff = jnp.clip(c[None, :] - c[:, None] + (NA_COLS - 1), 0, 2 * NA_COLS - 2)
    bias = rpb[:, roff[:, None, :, None], coff[None, :, None, :]]
    s = s + bias[None].astype(jnp.float32)
    s = jnp.where(col_ok[:, None, :], s, NEG)
    sh = s.shape
    p = jax.nn.softmax(s.reshape(sh[:4] + (kr * GRID_W,)), axis=-1).reshape(sh)
    o = jnp.einsum('bhrqkw,brkwhd->brqhd', p.astype(v.dtype), vb)
    return o.reshape(B, S, H, D)

def even_mixer(h, w_in, rpb, w_out, t5_table):
    B, S, _ = h.shape
    proj = h @ w_in
    a_part = proj[..., :3 * A_HEADS * HEAD_DIM]
    b_part = proj[..., 3 * A_HEADS * HEAD_DIM:]
    qa, ka, va = [t.reshape(B, S, A_HEADS, HEAD_DIM) for t in jnp.split(a_part, 3, axis=-1)]
    qb, kb, vb = [t.reshape(B, S, B_HEADS, HEAD_DIM) for t in jnp.split(b_part, 3, axis=-1)]
    oa = dilated_mixture(qa, ka, va, t5_table)
    ob = neighbourhood_attention(qb, kb, vb, rpb)
    o = jnp.concatenate([oa.reshape(B, S, -1), ob.reshape(B, S, -1)], axis=-1)
    return o @ w_out

def rotate(x, cos, sin):
    half = x.shape[-1] // 2
    x1, x2 = x[..., :half], x[..., half:]
    return jnp.concatenate([x1 * cos - x2 * sin, x1 * sin + x2 * cos], axis=-1)

def mla_mixer(h, w_in, q_norm, w_uq, kv_norm, w_uk, w_uv, w_out, t5_table):
    B, S, _ = h.shape
    H = C_HEADS
    proj = h @ w_in
    cq = rmsnorm(proj[..., :Q_LORA], q_norm)
    ckv = rmsnorm(proj[..., Q_LORA:Q_LORA + KV_LORA], kv_norm)
    kr = proj[..., Q_LORA + KV_LORA:]

    pos = jnp.arange(S, dtype=jnp.float32)
    freqs = ROPE_THETA ** (-jnp.arange(0, QK_ROPE, 2, dtype=jnp.float32) / QK_ROPE)
    ang = pos[:, None] * freqs[None, :]
    cos = jnp.cos(ang).astype(h.dtype)
    sin = jnp.sin(ang).astype(h.dtype)

    q = (cq @ w_uq).reshape(B, S, H, QK_NOPE + QK_ROPE)
    q_nope = q[..., :QK_NOPE]
    q_rope = rotate(q[..., QK_NOPE:], cos[None, :, None], sin[None, :, None])
    k_rope = rotate(kr, cos[None], sin[None])
    k_nope = (ckv @ w_uk).reshape(B, S, H, QK_NOPE)
    v = (ckv @ w_uv).reshape(B, S, H, V_DIM)
    scale = (QK_NOPE + QK_ROPE) ** -0.5

    nb = S // Q_BLOCK
    qn_blocks = q_nope.reshape(B, nb, Q_BLOCK, H, QK_NOPE).transpose(1, 0, 2, 3, 4)
    qr_blocks = q_rope.reshape(B, nb, Q_BLOCK, H, QK_ROPE).transpose(1, 0, 2, 3, 4)
    kpos = jnp.arange(S)

    def block(args):
        qn, qr, i = args
        s = (jnp.einsum('bqhd,bkhd->bhqk', qn, k_nope)
             + jnp.einsum('bqhd,bkd->bhqk', qr, k_rope)).astype(jnp.float32) * scale
        qpos = i * Q_BLOCK + jnp.arange(Q_BLOCK)
        s = s + t5_bias(t5_table, kpos[None, :] - qpos[:, None], H)[None]
        p = jax.nn.softmax(s, axis=-1)
        return jnp.einsum('bhqk,bkhd->bqhd', p.astype(v.dtype), v)

    o = lax.map(block, (qn_blocks, qr_blocks, jnp.arange(nb)))
    o = o.transpose(1, 0, 2, 3, 4).reshape(B, S, H * V_DIM)
    return o @ w_out

def swiglu(h, w_gate, w_up, w_down):
    return (jax.nn.silu(h @ w_gate) * (h @ w_up)) @ w_down

def setup_inputs(seed: int = 0) -> dict:
    key = jax.random.key(seed)
    ks = jax.random.split(key, 20)
    f32 = jnp.float32

    def w(k, shape, fan_in):
        return jax.random.normal(k, shape, f32) * (fan_in ** -0.5)

    def gain(k, shape):
        return 1.0 + 0.01 * jax.random.normal(k, shape, f32)

    mix_a_b = (A_HEADS + B_HEADS) * HEAD_DIM
    return {
        "x": jax.random.normal(ks[0], (BATCH, SEQ, D_MODEL), f32),
        "t5_table": 0.1 * jax.random.normal(ks[1], (T5_BUCKETS, T5_HEADS), f32),
        "attn_norm": gain(ks[2], (DEPTH, D_MODEL)),
        "ffn_norm": gain(ks[3], (DEPTH, D_MODEL)),
        "even_w_in": w(ks[4], (N_EVEN, D_MODEL, 3 * mix_a_b), D_MODEL),
        "na_rpb": 0.1 * jax.random.normal(ks[5], (N_EVEN, B_HEADS, 2 * NA_ROWS - 1, 2 * NA_COLS - 1), f32),
        "even_w_out": w(ks[6], (N_EVEN, mix_a_b, D_MODEL), mix_a_b),
        "odd_w_in": w(ks[7], (N_ODD, D_MODEL, Q_LORA + KV_LORA + QK_ROPE), D_MODEL),
        "mla_q_norm": gain(ks[8], (N_ODD, Q_LORA)),
        "mla_w_uq": w(ks[9], (N_ODD, Q_LORA, C_HEADS * (QK_NOPE + QK_ROPE)), Q_LORA),
        "mla_kv_norm": gain(ks[10], (N_ODD, KV_LORA)),
        "mla_w_uk": w(ks[11], (N_ODD, KV_LORA, C_HEADS * QK_NOPE), KV_LORA),
        "mla_w_uv": w(ks[12], (N_ODD, KV_LORA, C_HEADS * V_DIM), KV_LORA),
        "odd_w_out": w(ks[13], (N_ODD, C_HEADS * V_DIM, D_MODEL), C_HEADS * V_DIM),
        "ffn_w_gate": w(ks[14], (DEPTH, D_MODEL, D_FF), D_MODEL),
        "ffn_w_up": w(ks[15], (DEPTH, D_MODEL, D_FF), D_MODEL),
        "ffn_w_down": w(ks[16], (DEPTH, D_FF, D_MODEL), D_FF),
        "final_norm": gain(ks[17], (D_MODEL,)),
    }

def reference(x, t5_table, attn_norm, ffn_norm, even_w_in, na_rpb, even_w_out,
              odd_w_in, mla_q_norm, mla_w_uq, mla_kv_norm, mla_w_uk, mla_w_uv, odd_w_out,
              ffn_w_gate, ffn_w_up, ffn_w_down, final_norm):
    for layer in range(DEPTH):
        h = rmsnorm(x, attn_norm[layer])
        if layer % 2 == 0:
            i = layer // 2
            x = x + even_mixer(h, even_w_in[i], na_rpb[i], even_w_out[i], t5_table)
        else:
            i = layer // 2
            x = x + mla_mixer(h, odd_w_in[i], mla_q_norm[i], mla_w_uq[i], mla_kv_norm[i],
                              mla_w_uk[i], mla_w_uv[i], odd_w_out[i], t5_table)
        h = rmsnorm(x, ffn_norm[layer])
        x = x + swiglu(h, ffn_w_gate[layer], ffn_w_up[layer], ffn_w_down[layer])
    return rmsnorm(x, final_norm)


_drawn_inputs = setup_inputs


def setup_inputs(seed=0):
    import zlib

    import numpy as np

    out = dict(_drawn_inputs(seed))
    spreads = {}
    factors = {'t5_table': 4.676,
     'attn_norm': 8.0,
     'ffn_norm': 5.646,
     'na_rpb': 4.706,
     'mla_q_norm': 8.0,
     'mla_kv_norm': 8.0,
     'final_norm': 5.748}
    for name, (base, spread) in spreads.items():
        noise = np.random.default_rng([zlib.crc32(name.encode()), seed]).standard_normal(out[name].shape)
        drawn = base * np.exp(spread * noise) if base else spread * noise
        out[name] = __import__('jax').numpy.asarray(drawn.astype(out[name].dtype))
    for name, factor in factors.items():
        out[name] = (out[name] * factor).astype(out[name].dtype)
    return out
```

```python
from contextlib import ExitStack

import concourse.bass as bass
from concourse import mybir

F32 = mybir.dt.float32
F32R = mybir.dt.float32r
ALU = mybir.AluOpType
ACT = mybir.ActivationFunctionType

P = 128
SEQ = 1024
DM = 1024
KT = DM // P
HALF = SEQ // 2
QB = SEQ // P
HD = 64
DFF = 2816
NA_PAIRS = 4
NC_PAIRS = 8
A_COLS = 3 * 8 * HD
QT, KVT, ROPE = 3, 1, 32
UQ = HD + ROPE
C_SCALE = float(UQ) ** -0.5
EPS = 1e-6
GRID = 64
NROW = 14
PADW = 128
BIG = 3.0e38
TW = SEQ + SEQ - P
REL = 2 * SEQ
NSTEP = 2 * QB
NFF = DFF // (2 * P)

SB0 = 0
TB_A = 2 * SEQ
TB_B = 2 * SEQ
OFF_B = TB_B + 2 * 2 * NROW * GRID
MASK_B = OFF_B + NROW * GRID
COS = TB_A + 2 * TW
SIN = COS + SEQ
ONEHOT, T5E, VREL, PADT = 0, 2 * SEQ, 4 * SEQ, 6 * SEQ


def b_window(i):
    if i < 2:
        return 0, 512, (6 - 2 * i) * GRID
    if i < 6:
        return 256 * (i // 2 - 1), 768, (NROW + 2 * (1 - i % 2)) * GRID
    return 512, 512, (14 - 2 * i) * GRID


def a_window(i):
    return 0, SEQ, (QB - 1 - i) * P


PAIR = {"red": 16, "ex": 16, "rc": 16, "nm": 16, "tp": 34, "hi": 34, "lo": 34, "pv": 8, "oc": 8,
        "oa": 8, "od0": 4, "od1": 4, "kq_hi": 6, "kq_lo": 6, "vt": 1}


def times(n, d):
    return {k: n * v for k, v in d.items()}


NORM = {"sq": 16, "sqm": 16, "sr": 2, "rr": 2, "nt": 16, "nh": 16, "nl": 16}
PROJ = {"st0": 4, "st1": 4, "whi": 8, "ws": 8, "sc": 8, "xa": 8, "nh": 8, "nl": 8, "ol0": 1, "ol1": 1,
        "xr0": 1, "xr1": 1}
FFN = {"st0": 3, "st1": 3, "whi": 6, "ws": 6, "sc": 8, "sl": 4, "pr": 4, "ah": 4, "al": 4, "dn": 16,
       "xa": 16}
EVEN = {**times(4, {**PAIR, "whi": 3, "ws": 3, "sc": 19}), "st0": 6, "st1": 6}
PHASES = [
    ("load", {"xt": 8, "xc": 8, "tv": 2, "tc": 6, "pk": 1}),
    ("norm_a0", NORM),
    ("attn_a", {**EVEN, "tb0": 4, "tb1": 4}),
    ("attn_b", {**EVEN, "of": 16, "bb": 16, "bm": 1}),
    ("proj_0", PROJ),
    ("norm_f0", NORM),
    ("ffn_0", times(NFF, FFN)),
    ("norm_a1", {**NORM, "pk": 1}),
    ("latent", {"st0": 3, "st1": 2, "whi": 5, "ws": 5, "sc": 5, "raw": 5, "sq": 8, "sqm": 8, "sr": 4,
                "rr": 4, "nt": 8, "nh": 8, "nl": 8, "cs": 2, "rp": 4, "kr_hi": 2, "kr_lo": 2}),
    ("attn_c", {**times(8, {**PAIR, "st0": 8, "whi": 1, "ws": 1, "sc": 20, "ra": 1, "rp": 4}),
                "tb0": 8, "tb1": 8}),
    ("proj_1", PROJ),
    ("norm_f1", NORM),
    ("ffn_1", times(NFF, FFN)),
    ("last", {"sq": 16, "sqm": 16, "sr": 2, "rr": 2, "nt": 16, "yt": 8, "yc": 8, "yo0": 4, "yo1": 4}),
]
PRIME = {"red": 16, "lo": 2, "oa": 2, "od0": 1, "od1": 1, "al": 2, "ws": 2, "sc": 20, "sqm": 2, "dn": 1,
         "bb": 1, "sl": 2, "pr": 2, "xa": 2}
DMAS = {"pk", "od0", "od1", "st0", "st1", "ol0", "ol1", "xr0", "xr1", "tb0", "tb1", "of", "bm", "cs",
        "yo0", "yo1"}


def count_bases():
    base, now = {}, dict(PRIME)
    for phase, incs in PHASES:
        base[phase] = dict(now)
        for k, v in incs.items():
            now[k] = now.get(k, 0) + v
    return base


BASE = count_bases()


def at(phase, sem, n, it=0, per=0):
    unit = 16 if sem in DMAS else 1
    v = (BASE[phase].get(sem, 0) + n) * unit
    return v if per == 0 else it * (per * unit) + v


def flipped(ap):
    return ap.rearrange("p (b c) -> p b c", c=P)[:, :, ::-1]


def blocks(ap):
    return ap.rearrange("p (b c) -> p b c", c=P)


def build(nc, x, t5, gains, w_even, rpb, w_even_out, w_odd, w_uq, w_uk, w_uv, w_odd_out, w_gate, w_up,
          w_down, eye, flip, onehot, cos, sin, mask_b, out):
    ctx = ExitStack()
    with ctx:
        def sb(name, shape, dt):
            return ctx.enter_context(nc.sbuf_tensor(name, shape, dt))

        xT = sb("xT", [P, KT * SEQ], F32)
        stage = sb("stage", [P, 2, KT * P], F32)
        row = sb("row", [P, SEQ], F32)
        rstd = sb("rstd", [P, SEQ], F32)
        hT = sb("hT", [P, 2, KT, SEQ], F32R)
        W = sb("W", [P, 3, 2, KT * P], F32R)
        qk = sb("qk", [P, 6, SEQ], F32R)
        vv = sb("vv", [P, QB, 2, P], F32R)
        pt = sb("pt", [P, 8 * SEQ], F32R)
        eye_t = sb("eye_t", [P, P], F32)
        flip_t = sb("flip_t", [P, P], F32)
        ones = sb("ones", [P, P], F32)
        gain = sb("gain", [P, 44], F32)
        eps = sb("eps", [P, 1], F32)
        mneg = sb("mneg", [P, 2], F32)
        den = sb("den", [P, 2], F32)
        rden = sb("rden", [P, 2], F32)
        o_lo = sb("o_lo", [HD, 2, 256], F32)
        o_out = sb("o_out", [HD, 2, 256], F32)

        x3 = xT[:, :].rearrange("p (j t) -> p j t", j=KT)
        PT = pt[:, :].rearrange("p (b s k q) -> p b s k q", b=2, s=2, k=QB)
        act = pt[:, 0:4 * SEQ].rearrange("p (f s t) -> p f s t", f=2, s=2)
        score = [xT[:, SB0 + b * SEQ:SB0 + (b + 1) * SEQ] for b in range(2)]
        psS = [ctx.enter_context(nc.psum_tensor(f"psS{b}", [P, SEQ], F32)) for b in range(2)]
        psD = [ctx.enter_context(nc.psum_tensor(f"psD{b}", [P, HALF], F32)) for b in range(4)]

        park = nc.dram_tensor("park", (P, KT * SEQ), F32, kind="Internal").ap()
        heads = nc.dram_tensor("heads", (DM, SEQ), F32, kind="Internal").ap()
        rel_a = nc.dram_tensor("rel_a", (8, REL), F32, kind="Internal").ap()
        rel_c = nc.dram_tensor("rel_c", (16, REL), F32, kind="Internal").ap()
        offs = nc.dram_tensor("offs", (8 * 15, PADW), F32, kind="Internal").ap()

        names = sorted({k for _, d in PHASES for k in d}
                       | {"const", "setup", "passed", "xl0", "xl1", "xl2", "xl3", "scr", "toh"})
        S = {k: ctx.enter_context(nc.semaphore("s_" + k)) for k in names}
        xin = [stage[:, 0, :], stage[:, 1, :], row[:, :], rstd[:, :]]

        def plain(eng):
            eng.sem_inc(S["passed"], 1)

        def whalf(w, s, k, c=P, n=P, off=0):
            return W[:, w, s, off + k * c:off + k * c + n]

        def latent_ops(e):
            q = [qk[:, 4 * e, :], qk[:, 4 * e + 1, :]]
            return q + ([qk[:, 2, :], qk[:, 3, :]] if e == 0 else [hT[:, 0, 4, :], hT[:, 1, 4, :]])

        block = ctx.enter_context(nc.Block())

        @block.sync
        def _(sp):
            sp.dma_start(xT[0:33, ONEHOT:ONEHOT + REL], onehot[:, :]).then_inc(S["toh"], 16)
            for t in range(4):
                sp.dma_start(xin[t], x[t * P:(t + 1) * P, :]).then_inc(S[f"xl{t}"], 16)
            sp.dma_start(eye_t[:, :], eye[:, :]).then_inc(S["const"], 16)
            sp.dma_start(flip_t[:, :], flip[:, :]).then_inc(S["const"], 16)
            sp.dma_start(gain[:, :], gains[:, :]).then_inc(S["const"], 16)
            sp.wait_ge(S["setup"], 4)
            sp.dma_start(xT[0:32, T5E:T5E + 16], t5[:, :]).then_inc(S["toh"], 16)
            sp.dma_start(xT[0:120, PADT + 48:PADT + 79], rpb[:, :]).then_inc(S["toh"], 16)
            sp.wait_ge(S["toh"], 48)
            sp.dma_start(offs[:, :], xT[0:120, PADT:PADT + PADW]).then_inc(S["scr"], 16)
            sp.wait_ge(S["tc"], at("load", "tc", 6))
            sp.dma_start(rel_a[:, :], xT[0:8, VREL:VREL + REL]).then_inc(S["scr"], 16)
            sp.dma_start(rel_c[:, :], xT[32:48, VREL:VREL + REL]).then_inc(S["scr"], 16)
            for t in range(4, 8):
                sp.wait_ge(S["xt"], t - 3)
                sp.dma_start(xin[t - 4], x[t * P:(t + 1) * P, :]).then_inc(S[f"xl{t - 4}"], 16)
            sp.wait_ge(S["xt"], 8)

            def load(ph, n, src, it=0, per=0):
                sp.wait_ge(S["ws"], at(ph, "ws", n - 1, it, per))
                plain(sp)
                k, c = src.shape[1], src.shape[2]
                sp.dma_start(stage[:, n % 2, 0:k * c].rearrange("p (k c) -> p k c", k=k), src)\
                    .then_inc(S[f"st{n % 2}"], 16)

            def even_pair(ph, it, p, col):
                for c, first in enumerate((8 * HD, 0, 16 * HD)):
                    w = w_even[:, bass.ds(it * (2 * P) + (col + p * P + first), P)]
                    load(ph, 3 * p + c, w.rearrange("(k p) c -> p k c", p=P), it, 6)

            def rel_table(rel, e, head):
                plain(sp)
                src = bass.AP(tensor=rel.tensor, offset=head * REL, ap=[[1, P], [1, TW]])
                sp.dma_start(xT[:, TB_A + e * TW:TB_A + (e + 1) * TW], src).then_inc(S[f"tb{e}"], 16)

            sp.wait_ge(S["scr"], 48)
            sp.wait_ge(S["pk"], at("load", "pk", 1))
            sp.wait_ge(S["nl"], at("norm_a0", "nl", 16))
            with sp.Fori(0, 2, 1) as it:
                for p in range(2):
                    even_pair("attn_a", it, p, 0)
                    for e in range(2):
                        sp.wait_ge(S["red"], at("attn_a", "red", 16 * p + 8 * e - 8, it, 32))
                        rel_table(rel_a, e, it * 4 + (2 * p + e))
            sp.wait_ge(S["lo"], at("attn_b", "lo", 0))
            sp.dma_start(xT[:, MASK_B:MASK_B + (NROW + 1) * GRID], mask_b[:, :]).then_inc(S["bm"], 16)
            with sp.Fori(0, 2, 1) as it:
                for p in range(2):
                    even_pair("attn_b", it, p, A_COLS)
                    for e in range(2):
                        sp.wait_ge(S["bb"], at("attn_b", "bb", 4 * p + 2 * e, it, 8))
                        plain(sp)
                        for d in range(2):
                            src = bass.AP(tensor=offs.tensor,
                                          offset=it * (4 * 15 * PADW) + ((2 * p + e) * 15 + d) * PADW,
                                          ap=[[1, GRID], [PADW, NROW], [1, GRID]])
                            dst = xT[d * GRID:(d + 1) * GRID, OFF_B:OFF_B + NROW * GRID]
                            sp.dma_start(dst.rearrange("p (r c) -> p r c", c=GRID), src)\
                                .then_inc(S["of"], 16)

            def proj_weights(ph, w):
                sp.wait_ge(S["ws"], at(ph, "ws", 0))
                with sp.Fori(0, 4, 1) as it:
                    for n in range(2):
                        src = w[:, bass.ds(it * (2 * P) + n * P, P)]
                        load(ph, n, src.rearrange("(k p) c -> p k c", p=P), it, 2)

            def ffn_weights(ph, layer):
                with sp.Fori(0, NFF, 1) as it:
                    n = 0
                    for f in range(2):
                        for w in (w_gate, w_up):
                            src = w[layer, :, bass.ds(it * (2 * P) + f * P, P)]
                            load(ph, n, src.rearrange("(k p) c -> p k c", p=P), it, 6)
                            n += 1
                    for f in range(2):
                        src = w_down[layer, bass.ds(it * (2 * P) + f * P, P), :]
                        load(ph, n, src.rearrange("p (k c) -> p k c", c=P), it, 6)
                        n += 1

            proj_weights("proj_0", w_even_out)
            ffn_weights("ffn_0", 0)
            for c in range(4):
                load("latent", c, w_odd[:, c * P:(c + 1) * P].rearrange("(k p) c -> p k c", p=P))
            load("latent", 4, w_odd[:, 4 * P:4 * P + ROPE].rearrange("(k p) c -> p k c", p=P))
            sp.wait_ge(S["pk"], at("norm_a1", "pk", 1))
            sp.wait_ge(S["nl"], at("norm_a1", "nl", 16))
            sp.dma_start(xT[:, COS:COS + SEQ], cos[:, :]).then_inc(S["cs"], 16)
            sp.dma_start(xT[:, SIN:SIN + SEQ], sin[:, :]).then_inc(S["cs"], 16)
            sp.wait_ge(S["kr_lo"], at("latent", "kr_lo", 2))
            uq = w_uq.rearrange("(k p) (h c) -> k p h c", p=P, c=UQ)
            with sp.Fori(0, NC_PAIRS, 1) as it:
                sp.wait_ge(S["ws"], at("attn_c", "ws", 0, it, 1))
                plain(sp)
                for k in range(QT):
                    sp.dma_start(stage[:, 0, k * P:(k + 1) * P].rearrange("p (h c) -> p h c", h=2),
                                 uq[k, :, bass.ds(it * 2, 2), 0:HD]).then_inc(S["st0"], 16)
                    o = QT * P + k * 2 * ROPE
                    sp.dma_start(stage[:, 0, o:o + 2 * ROPE].rearrange("p (h c) -> p h c", h=2),
                                 uq[k, :, bass.ds(it * 2, 2), HD:UQ]).then_inc(S["st0"], 16)
                o = QT * (P + 2 * ROPE)
                sp.dma_start(stage[:, 0, o:o + P], w_uk[:, bass.ds(it * P, P)]).then_inc(S["st0"], 16)
                sp.dma_start(stage[:, 0, o + P:o + 2 * P], w_uv[:, bass.ds(it * P, P)])\
                    .then_inc(S["st0"], 16)
                for e in range(2):
                    sp.wait_ge(S["red"], at("attn_c", "red", 8 * e - 8, it, 16))
                    rel_table(rel_c, e, it * 2 + e)
            proj_weights("proj_1", w_odd_out)
            ffn_weights("ffn_1", 1)
            for t in range(QB):
                sp.wait_ge(S["yc"], at("last", "yc", t + 1))
                sp.dma_start(out[t * P:(t + 1) * P, :], stage[:, t % 2, :]).then_inc(S[f"yo{t % 2}"], 16)
            for b in range(2):
                sp.wait_ge(S[f"yo{b}"], at("last", f"yo{b}", 4))

        @block.gpsimd
        def _(pool):
            for k, v in PRIME.items():
                pool.sem_inc(S[k], v * (16 if k in DMAS else 1))
            pool.memset(xT[0:33, T5E:T5E + 16], 1.0).then_inc(S["setup"], 1)
            pool.memset(xT[0:120, PADT:PADT + PADW], 0.0).then_inc(S["setup"], 1)
            pool.memset(ones[:, :], 1.0).then_inc(S["setup"], 1)
            pool.memset(eps[:, :], EPS).then_inc(S["setup"], 1)

            def split(ph, n, w, free, it=0, per=0, cols=KT * P, dmas=1, buf=None):
                b = n % 2 if buf is None else buf
                same = [j for j in range(n + 1) if j % 2 == b]
                half = sum(1 for j in range(per) if j % 2 == b) if buf is None else 1
                pool.wait_ge(S[f"st{b}"], at(ph, f"st{b}", dmas * len(same) if buf is None else dmas,
                                             it, half * dmas))
                if free:
                    pool.wait_ge(S[free[0]], at(ph, free[0], free[1], it, free[2]))
                src, hi, lo = stage[:, b, 0:cols], W[:, w, 0, 0:cols], W[:, w, 1, 0:cols]
                plain(pool)
                pool.tensor_copy(hi, src).then_inc(S["whi"], 1)
                pool.wait_ge(S["whi"], at(ph, "whi", n + 1, it, per))
                pool.tensor_tensor(lo, src, hi.bitcast(F32), ALU.subtract).then_inc(S["ws"], 1)

            def even_weights(ph):
                with pool.Fori(0, 2, 1) as it:
                    for n in range(6):
                        split(ph, n, n % 3, ("sc", 19 * (n // 3) + n % 3 + 1 - 19, 38), it, 6)

            def proj_weights(ph):
                with pool.Fori(0, 4, 1) as it:
                    for n in range(2):
                        split(ph, n, n, ("sc", n - 1, 2), it, 2)

            def ffn_weights(ph):
                slots = [(0, ("sc", 0, 8)), (1, ("dn", 0, 16)), (2, ("dn", 0, 16)),
                         (0, ("sc", 2, 8)), (1, ("sc", 4, 8)), (2, ("sc", 6, 8))]
                with pool.Fori(0, NFF, 1) as it:
                    for n, (w, free) in enumerate(slots):
                        split(ph, n, w, free, it, 6)

            even_weights("attn_a")
            even_weights("attn_b")
            pool.wait_ge(S["sc"], at("proj_0", "sc", 19 - 3 - NSTEP))
            proj_weights("proj_0")
            pool.wait_ge(S["sc"], at("ffn_0", "sc", 0))
            ffn_weights("ffn_0")
            pool.wait_ge(S["dn"], at("latent", "dn", 0))
            for n in range(5):
                split("latent", n, n % 3, ("sc", n - 2, 0) if n >= 3 else None,
                      cols=KT * P if n < 4 else KT * ROPE)
            pool.wait_ge(S["sc"], at("attn_c", "sc", 0))
            with pool.Fori(0, NC_PAIRS, 1) as it:
                split("attn_c", 0, 0, ("sc", 4 - 20, 20), it, 1, cols=QT * (P + 2 * ROPE) + 2 * P, dmas=8, buf=0)
            pool.wait_ge(S["sc"], at("proj_1", "sc", 4 - 20))
            proj_weights("proj_1")
            pool.wait_ge(S["sc"], at("ffn_1", "sc", 0))
            ffn_weights("ffn_1")

        @block.tensor
        def _(pe):
            def product(ps, h, ks, wop, rhs):
                o = ps[:, h * HALF:(h + 1) * HALF]
                for n, k in enumerate(ks):
                    pe.matmul(o, wop(0, k), rhs(0, k, h), start=n == 0, stop=False)
                    pe.matmul(o, wop(0, k), rhs(1, k, h), start=False, stop=False)
                    mm = pe.matmul(o, wop(1, k), rhs(0, k, h), start=False, stop=n == len(ks) - 1)
                return mm

            def h_of(s, k, h):
                return hT[:, s, k, h * HALF:(h + 1) * HALF]

            def mean_square(ph, tiles):
                u = 0
                for j0 in tiles:
                    for h in range(2):
                        for j in range(j0):
                            pe.wait_ge(S["sq"], at(ph, "sq", u + 1))
                            pe.matmul(psD[h][:, :], ones[:, :], row[:, (u % 2) * HALF:(u % 2 + 1) * HALF],
                                      start=j == 0, stop=j == j0 - 1).then_inc(S["sqm"], 1)
                            u += 1
                        if len(tiles) > 1 and h == 1:
                            pe.wait_ge(S["sr"], at(ph, "sr", 2 if j0 == tiles[0] else 4))

            pe.wait_ge(S["toh"], 48)
            for c in range(4):
                mm = pe.matmul(psS[c // 2][0:8, (c % 2) * HALF:(c % 2 + 1) * HALF],
                               xT[0:33, T5E:T5E + 8], xT[0:33, ONEHOT + c * HALF:ONEHOT + (c + 1) * HALF],
                               start=True, stop=True)
            mm.then_inc(S["tv"], 1)
            for c in range(4):
                mm = pe.matmul(psD[c][0:16, :], xT[0:32, T5E:T5E + 16],
                               xT[0:32, ONEHOT + c * HALF:ONEHOT + (c + 1) * HALF], start=True, stop=True)
            mm.then_inc(S["tv"], 1)
            pe.wait_ge(S["const"], 48)
            pe.wait_ge(S["tc"], at("load", "tc", 2))
            for t in range(QB):
                pe.wait_ge(S[f"xl{t % 4}"], 16 * (t // 4 + 1))
                if t >= 2:
                    pe.wait_ge(S["xc"], at("load", "xc", t - 1))
                for j in range(KT):
                    mm = pe.transpose(psS[t % 2][:, j * P:(j + 1) * P], xin[t % 4][:, j * P:(j + 1) * P],
                                      eye_t[:, :])
                mm.then_inc(S["xt"], 1)
            pe.wait_ge(S["setup"], 4)
            mean_square("norm_a0", [KT])

            def attention(ph, it, nsc, window, operands, k_of, first, ready, bank0):
                for t in range(NSTEP + 3):
                    if t < NSTEP:
                        e, i = t // QB, t % QB
                        k0, nk, _ = window(i)
                        if t in first:
                            for sem, n, per in first[t]:
                                pe.wait_ge(S[sem], at(ph, sem, n, it, per))
                        if t >= 2:
                            pe.wait_ge(S["red"], at(ph, "red", t - 1, it, 16))
                        ops = operands(e, i)
                        ps = psS[(t + bank0) % 2]
                        for c in range(0, nk, HALF):
                            w = min(HALF, nk - c)
                            for n, (q, k) in enumerate(ops):
                                mm = pe.matmul(ps[:, c:c + w], q, k[:, k0 + c:k0 + c + w],
                                               start=n == 0, stop=n == len(ops) - 1)
                        mm.then_inc(S["sc"], 1)
                    if 2 <= t < NSTEP + 2:
                        u = t - 2
                        nt = window(u % QB)[1] // P
                        pe.wait_ge(S["nm"], at(ph, "nm", u + 1, it, 16))
                        cut = (nt + 1) // 2
                        for b, (j0, j1) in enumerate(((0, cut), (cut, nt))):
                            pe.wait_ge(S["lo"], at(ph, "lo", 2 + 2 * u + b - 1, it, 34))
                            for j in range(j0, j1):
                                mm = pe.transpose(psD[b][:, (j - j0) * P:(j - j0 + 1) * P],
                                                  score[u % 2][:, j * P:(j + 1) * P], flip_t[:, :])
                            mm.then_inc(S["tp"], 1)
                    if t >= 4 and t % 2 == 0 or t == NSTEP + 2:
                        g = (t - 4) // 2
                        if g < QB:
                            e = g // 4
                            k0, nk, _ = window((2 * g) % QB)
                            pe.wait_ge(S["lo"], at(ph, "lo", 2 + 4 * g + 4, it, 34))
                            pe.wait_ge(S["oa"], at(ph, "oa", g - 1, it, 8))
                            n = 0
                            for j in range(nk // P):
                                for s in range(2):
                                    mm = pe.matmul(psD[2 + g % 2][:, 0:256], vv[:, k0 // P + j, e, :],
                                                   PT[:, g % 2, s, j, :], start=n == 0,
                                                   stop=n == 2 * nk // P - 1)
                                    n += 1
                            mm.then_inc(S["pv"], 1)

            def turn_v(ph, it):
                pe.wait_ge(S["vt"], at(ph, "vt", 1, it, 1))
                for b in range(2):
                    pe.wait_ge(S["lo"], at(ph, "lo", b - 1, it, 34))
                    for j in range(4):
                        o = (4 * b + j) * P
                        mm = pe.transpose(psD[b][:, j * P:(j + 1) * P], row[:, o:o + P], eye_t[:, :])
                    mm.then_inc(S["tp"], 1)

            def even_operands(e, i):
                q = qk[:, 3 * e, i * P:(i + 1) * P]
                return [(q, qk[:, 3 * e + 1, :]), (q, qk[:, 3 * e + 2, :])]

            def even_phase(ph, norm, window):
                with pe.Fori(0, 4, 1) as it:
                    for c, (ps, wait) in enumerate(((0, ("red", 0, 16)), (1, ("red", 0, 16)),
                                                    (0, ("kq_lo", 4, 6)))):
                        pe.wait_ge(S["ws"], at(ph, "ws", c + 1, it, 3))
                        pe.wait_ge(S[wait[0]], at(ph, wait[0], wait[1], it, wait[2]))
                        for h in range(2):
                            if norm and c == 0:
                                pe.wait_ge(S["nl"], at(norm, "nl", 8 * (h + 1)))
                            mm = product(psS[ps], h, range(KT), lambda s, k, c=c: whalf(c, s, k), h_of)
                        mm.then_inc(S["sc"], 1)
                    turn_v(ph, it)
                    attention(ph, it, 19, window, even_operands, None,
                              {0: [("kq_lo", 6, 6)], 1: [("vt", 1, 1)]}, None, 1)

            even_phase("attn_a", "norm_a0", a_window)
            even_phase("attn_b", None, b_window)

            def proj(ph):
                pe.wait_ge(S["nl"], at(ph, "nl", 8))
                with pe.Fori(0, 4, 1) as it:
                    for n in range(2):
                        pe.wait_ge(S["ws"], at(ph, "ws", n + 1, it, 2))
                        pe.wait_ge(S["xa"], at(ph, "xa", n - 1, it, 2))
                        for h in range(2):
                            mm = product(psS[n], h, range(KT), lambda s, k, n=n: whalf(n, s, k), h_of)
                        mm.then_inc(S["sc"], 1)

            def ffn(ph, norm):
                with pe.Fori(0, NFF, 1) as it:
                    for f in range(2):
                        for g in range(2):
                            n = 2 * f + g
                            pe.wait_ge(S["ws"], at(ph, "ws", n + 1, it, 6))
                            for h in range(2):
                                if n == 0:
                                    pe.wait_ge(S["nl"], at(norm, "nl", 8 * (h + 1)))
                                sem = "pr" if g else "sl"
                                pe.wait_ge(S[sem], at(ph, sem, 2 * f + h - 1, it, 4))
                                product(psS[g], h, range(KT), lambda s, k, w=n % 3: whalf(w, s, k), h_of)\
                                    .then_inc(S["sc"], 1)
                    pe.wait_ge(S["ws"], at(ph, "ws", 6, it, 6))
                    for h in range(2):
                        pe.wait_ge(S["al"], at(ph, "al", 3 + h, it, 4))
                        for m in range(KT):
                            n = h * KT + m
                            pe.wait_ge(S["xa"], at(ph, "xa", n - 3, it, 16))
                            o = psD[n % 4][:, :]
                            for f in range(2):
                                c = h * HALF
                                pe.matmul(o, whalf(1 + f, 0, m), act[:, f, 0, c:c + HALF],
                                          start=f == 0, stop=False)
                                pe.matmul(o, whalf(1 + f, 0, m), act[:, f, 1, c:c + HALF],
                                          start=False, stop=False)
                                mm = pe.matmul(o, whalf(1 + f, 1, m), act[:, f, 0, c:c + HALF],
                                               start=False, stop=f == 1)
                            mm.then_inc(S["dn"], 1)

            proj("proj_0")
            pe.wait_ge(S["xa"], at("norm_f0", "xa", 0))
            mean_square("norm_f0", [KT])
            ffn("ffn_0", "norm_f0")
            pe.wait_ge(S["xa"], at("norm_a1", "xa", 0))
            mean_square("norm_a1", [KT])
            for c in range(5):
                pe.wait_ge(S["ws"], at("latent", "ws", c + 1))
                if c >= 2:
                    pe.wait_ge(S["raw"], at("latent", "raw", c - 1))
                for h in range(2):
                    if c == 0:
                        pe.wait_ge(S["nl"], at("norm_a1", "nl", 8 * (h + 1)))
                    mm = product(psS[c % 2], h, range(KT),
                                 lambda s, k, c=c: whalf(c % 3, s, k, P if c < 4 else ROPE), h_of)
                mm.then_inc(S["sc"], 1)
            mean_square("latent", [QT, KVT])

            def latent_pair_ops(e, i):
                qh, ql, kh, kl = latent_ops(e)
                b = slice(i * P, (i + 1) * P)
                return [(qh[0:UQ, b], kh[0:UQ, :]), (qh[0:UQ, b], kl[0:UQ, :]), (ql[0:UQ, b], kh[0:UQ, :])]

            pe.wait_ge(S["nl"], at("latent", "nl", 8))
            pe.wait_ge(S["kr_lo"], at("latent", "kr_lo", 2))
            o_r, o_k, o_v = QT * P, QT * (P + 2 * ROPE), QT * (P + 2 * ROPE) + P
            with pe.Fori(0, NC_PAIRS, 1) as it:
                ph = "attn_c"
                pe.wait_ge(S["ws"], at(ph, "ws", 1, it, 1))
                pe.wait_ge(S["red"], at(ph, "red", 0, it, 16))
                for ks, ps, wop, wait in (
                        ((3,), 0, lambda s, k: whalf(0, s, 0, off=o_k), None),
                        (range(QT), 1, lambda s, k: whalf(0, s, k), None),
                        ((3,), 0, lambda s, k: whalf(0, s, 0, off=o_v), ("kq_lo", 2, 6)),
                        (range(QT), 1, lambda s, k: whalf(0, s, k, 2 * ROPE, off=o_r), ("kq_lo", 4, 6))):
                    if wait:
                        pe.wait_ge(S[wait[0]], at(ph, wait[0], wait[1], it, wait[2]))
                    for h in range(2):
                        mm = product(psS[ps], h, ks, wop, h_of)
                    mm.then_inc(S["sc"], 1)
                turn_v(ph, it)
                attention(ph, it, 20, lambda i: a_window(i), latent_pair_ops, None,
                          {0: [("vt", 1, 1), ("kq_lo", 6, 6)]}, None, 0)
            proj("proj_1")
            pe.wait_ge(S["xa"], at("norm_f1", "xa", 0))
            mean_square("norm_f1", [KT])
            ffn("ffn_1", "norm_f1")
            pe.wait_ge(S["xa"], at("last", "xa", 0))
            mean_square("last", [KT])
            for t in range(QB):
                if t % 4 == 0:
                    pe.wait_ge(S["nt"], at("last", "nt", 8 * (t // 4 + 1)))
                if t >= 2:
                    pe.wait_ge(S["yc"], at("last", "yc", t - 1))
                for j in range(KT):
                    mm = pe.transpose(psS[t % 2][:, j * P:(j + 1) * P], x3[:, j, t * P:(t + 1) * P],
                                      eye_t[:, :])
                mm.then_inc(S["yt"], 1)

        @block.scalar
        def _(sc):
            def square(ph, u, src):
                sc.wait_ge(S["sqm"], at(ph, "sqm", u - 1))
                sc.activation(row[:, (u % 2) * HALF:(u % 2 + 1) * HALF], src, ACT.Square)\
                    .then_inc(S["sq"], 1)

            def root(ph, n, u, h, width):
                sc.wait_ge(S["sqm"], at(ph, "sqm", u))
                sc.activation(rstd[:, h * HALF:(h + 1) * HALF], psD[h][:, :], ACT.Sqrt,
                              bias=eps[:, 0:1], scale=1.0 / width).then_inc(S["sr"], 1)

            def keep_hi(ph, u, j, h):
                sc.wait_ge(S["nt"], at(ph, "nt", u + 1))
                sc.activation(hT[:, 0, j, h * HALF:(h + 1) * HALF], psD[2 + u % 2][:, :], ACT.Copy)\
                    .then_inc(S["nh"], 1)

            def norm(ph, keep=True):
                for j in range(KT):
                    square(ph, j, x3[:, j, 0:HALF])
                root(ph, 0, KT, 0, DM)
                for j in range(KT):
                    square(ph, KT + j, x3[:, j, HALF:SEQ])
                    if keep:
                        keep_hi(ph, j, j, 0)
                root(ph, 1, 2 * KT, 1, DM)
                if keep:
                    for j in range(KT):
                        keep_hi(ph, KT + j, j, 1)

            sc.wait_ge(S["xc"], at("load", "xc", 8))
            sc.wait_ge(S["setup"], 4)
            sc.dma_start(park[:, :], xT[:, :]).then_inc(S["pk"], 16)
            norm("norm_a0")

            def attention(ph, it, nsc, window, nfix, pair0):
                for t in range(NSTEP + 5):
                    if t < NSTEP:
                        nk = window(t % QB)[1]
                        sc.wait_ge(S["red"], at(ph, "red", t + 1, it, 16))
                        s = score[t % 2][:, 0:nk]
                        sc.activation(s, s, ACT.Exp, bias=mneg[:, t % 2:t % 2 + 1], scale=-1.0,
                                      accum_out=den[:, t % 2:t % 2 + 1]).then_inc(S["ex"], 1)
                    if 2 <= t < NSTEP + 2:
                        u = t - 2
                        nt = window(u % QB)[1] // P
                        cut = (nt + 1) // 2
                        g, q = u // 2, (u % 2) * P
                        for b, (j0, j1) in enumerate(((0, cut), (cut, nt))):
                            sc.wait_ge(S["tp"], at(ph, "tp", 2 + 2 * u + b + 1, it, 34))
                            if g >= 2:
                                sc.wait_ge(S["pv"], at(ph, "pv", g - 1, it, 8))
                            sc.activation(PT[:, g % 2, 0, j0:j1, q:q + P],
                                          blocks(psD[b][:, 0:(j1 - j0) * P]), ACT.Copy).then_inc(S["hi"], 1)
                    if t >= 5 and t % 2 == 1:
                        g = (t - 5) // 2
                        if g < QB:
                            sc.wait_ge(S["pv"], at(ph, "pv", g + 1, it, 8))
                            sc.wait_ge(S["oa"], at(ph, "oa", g - 1, it, 8))
                            sc.activation(o_lo[:, g % 2, :], psD[2 + g % 2][HD:P, 0:256], ACT.Copy)\
                                .then_inc(S["oc"], 1)
                    if t >= 6 and t % 2 == 0:
                        g = (t - 6) // 2
                        if g < QB:
                            store_head(ph, it, g, pair0)

            def store_head(ph, it, g, pair0):
                e, c = g // 4, (g % 4) * 256
                sc.wait_ge(S["oa"], at(ph, "oa", g + 1, it, 8))
                sc.dma_start(heads[bass.ds(it * P + (pair0 * P + e * HD), HD), c:c + 256],
                             o_out[:, g % 2, :]).then_inc(S[f"od{g % 2}"], 16)

            def keep_v(ph, it):
                for b in range(2):
                    sc.wait_ge(S["tp"], at(ph, "tp", b + 1, it, 34))
                    sc.activation(vv[:, 4 * b:4 * b + 4, :, 0:HD],
                                  psD[b][:, :].rearrange("p (k e d) -> p k e d", k=4, e=2), ACT.Copy)\
                        .then_inc(S["hi"], 1)

            def even_phase(ph, window, pair0):
                with sc.Fori(0, 4, 1) as it:
                    sc.wait_ge(S["sc"], at(ph, "sc", 1, it, 19))
                    for e in range(2):
                        for d in range(2):
                            sc.activation(qk[d * HD:(d + 1) * HD, 3 * e + 1, :],
                                          psS[0][e * HD:(e + 1) * HD, :], ACT.Copy).then_inc(S["kq_hi"], 1)
                    sc.wait_ge(S["sc"], at(ph, "sc", 2, it, 19))
                    for e in range(2):
                        sc.activation(flipped(qk[0:HD, 3 * e, :]), blocks(psS[1][e * HD:(e + 1) * HD, :]),
                                      ACT.Copy, scale=HD ** -0.5).then_inc(S["kq_hi"], 1)
                    sc.wait_ge(S["sc"], at(ph, "sc", 3, it, 19))
                    sc.activation(row[:, :], psS[0][:, :], ACT.Copy).then_inc(S["vt"], 1)
                    keep_v(ph, it)
                    attention(ph, it, 19, window, 3, pair0)

            even_phase("attn_a", a_window, 0)
            even_phase("attn_b", b_window, 4)

            def gather_heads(ph):
                for b in range(2):
                    sc.wait_ge(S[f"od{b}"], at(ph, f"od{b}", 0))
                sc.wait_ge(S["lo"], at(ph, "lo", 0))
                h3 = heads.rearrange("(j p) t -> p j t", p=P)
                for b in range(2):
                    sc.dma_start(x3[:, 4 * b:4 * b + 4, :], h3[:, 4 * b:4 * b + 4, :])\
                        .then_inc(S[f"ol{b}"], 16)
                for j in range(KT):
                    if j % 4 == 0:
                        sc.wait_ge(S[f"ol{j // 4}"], at(ph, f"ol{j // 4}", 1))
                    sc.activation(hT[:, 0, j, :], x3[:, j, :], ACT.Copy).then_inc(S["nh"], 1)
                for b in range(2):
                    sc.wait_ge(S["nl"], at(ph, "nl", 4 * b + 4))
                    sc.dma_start(x3[:, 4 * b:4 * b + 4, :],
                                 park[:, 4 * b * SEQ:(4 * b + 4) * SEQ].rearrange("p (j t) -> p j t", j=4))\
                        .then_inc(S[f"xr{b}"], 16)

            def ffn(ph):
                with sc.Fori(0, NFF, 1) as it:
                    for f in range(2):
                        for h in range(2):
                            c = slice(h * HALF, (h + 1) * HALF)
                            sc.wait_ge(S["sc"], at(ph, "sc", 4 * f + h + 1, it, 8))
                            sc.wait_ge(S["al"], at(ph, "al", 2 * f + h - 1, it, 4))
                            sc.activation(row[:, c], psS[0][:, c], ACT.Silu).then_inc(S["sl"], 1)
                        for h in range(2):
                            c = slice(h * HALF, (h + 1) * HALF)
                            sc.wait_ge(S["pr"], at(ph, "pr", 2 * f + h + 1, it, 4))
                            sc.activation(act[:, f, 0, c], row[:, c], ACT.Copy).then_inc(S["ah"], 1)

            gather_heads("proj_0")
            sc.wait_ge(S["xa"], at("norm_f0", "xa", 0))
            norm("norm_f0")
            ffn("ffn_0")
            sc.wait_ge(S["xa"], at("norm_a1", "xa", 0))
            sc.dma_start(park[:, :], xT[:, :]).then_inc(S["pk"], 16)
            norm("norm_a1")
            sc.wait_ge(S["pk"], at("norm_a1", "pk", 1))
            sc.wait_ge(S["nl"], at("norm_a1", "nl", 16))
            for c in range(5):
                sc.wait_ge(S["sc"], at("latent", "sc", c + 1))
                sc.activation(x3[:, c, :], psS[c % 2][:, :], ACT.Copy).then_inc(S["raw"], 1)
            sc.wait_ge(S["raw"], at("latent", "raw", 5))
            u = n = 0
            for j0, nj in ((0, QT), (QT, KVT)):
                for h in range(2):
                    for j in range(nj):
                        square("latent", u, x3[:, j0 + j, h * HALF:(h + 1) * HALF])
                        u += 1
                    if n >= 2:
                        sc.wait_ge(S["nt"], at("latent", "nt", QT * (n - 1)))
                    root("latent", n, u, h, nj * P)
                    n += 1
                if j0 == 0:
                    for v in range(2 * QT):
                        keep_hi("latent", v, v % QT, v // QT)
            for v in range(2):
                keep_hi("latent", 2 * QT + v, QT, v)
            sc.wait_ge(S["rp"], at("latent", "rp", 4))
            for e in range(2):
                sc.activation(latent_ops(e)[2][HD:UQ, :], psS[1][0:ROPE, :], ACT.Copy)\
                    .then_inc(S["kr_hi"], 1)
            with sc.Fori(0, NC_PAIRS, 1) as it:
                ph = "attn_c"
                sc.wait_ge(S["sc"], at(ph, "sc", 1, it, 20))
                for e in range(2):
                    sc.activation(latent_ops(e)[2][0:HD, :], psS[0][e * HD:(e + 1) * HD, :], ACT.Copy)\
                        .then_inc(S["kq_hi"], 1)
                sc.wait_ge(S["sc"], at(ph, "sc", 2, it, 20))
                for e in range(2):
                    sc.activation(flipped(latent_ops(e)[0][0:HD, :]), blocks(psS[1][e * HD:(e + 1) * HD, :]),
                                  ACT.Copy, scale=C_SCALE).then_inc(S["kq_hi"], 1)
                sc.wait_ge(S["sc"], at(ph, "sc", 3, it, 20))
                sc.activation(row[:, :], psS[0][:, :], ACT.Copy).then_inc(S["vt"], 1)
                sc.wait_ge(S["sc"], at(ph, "sc", 4, it, 20))
                sc.activation(rstd[0:HD, :], psS[1][0:HD, :], ACT.Copy, scale=C_SCALE)\
                    .then_inc(S["ra"], 1)
                keep_v(ph, it)
                sc.wait_ge(S["rp"], at(ph, "rp", 4, it, 4))
                for e in range(2):
                    sc.activation(flipped(latent_ops(e)[0][HD:UQ, :]),
                                  blocks(psS[1][e * ROPE:(e + 1) * ROPE, :]), ACT.Copy)\
                        .then_inc(S["kq_hi"], 1)
                attention(ph, it, 20, a_window, 4, 0)
            gather_heads("proj_1")
            sc.wait_ge(S["xa"], at("norm_f1", "xa", 0))
            norm("norm_f1")
            ffn("ffn_1")
            sc.wait_ge(S["xa"], at("last", "xa", 0))
            norm("last", keep=False)

        @block.vector
        def _(ve):
            ve.wait_ge(S["tv"], 1)
            for b in range(2):
                ve.tensor_copy(xT[0:8, VREL + b * SEQ:VREL + (b + 1) * SEQ], psS[b][0:8, :])\
                    .then_inc(S["tc"], 1)
            ve.wait_ge(S["tv"], 2)
            for c in range(4):
                ve.tensor_copy(xT[32:48, VREL + c * HALF:VREL + (c + 1) * HALF], psD[c][0:16, :])\
                    .then_inc(S["tc"], 1)
            ve.wait_ge(S["scr"], 48)
            for t in range(QB):
                ve.wait_ge(S["xt"], t + 1)
                ve.tensor_copy(x3[:, :, t * P:(t + 1) * P], blocks(psS[t % 2][:, :])).then_inc(S["xc"], 1)

            def reciprocal(ph, n, h):
                ve.wait_ge(S["sr"], at(ph, "sr", n + 1))
                r = rstd[:, h * HALF:(h + 1) * HALF]
                ve.reciprocal(r, r).then_inc(S["rr"], 1)
                ve.wait_ge(S["rr"], at(ph, "rr", n + 1))

            def scaled(ph, u, h, src, g):
                ve.scalar_tensor_tensor(psD[2 + u % 2][:, :], src[:, h * HALF:(h + 1) * HALF],
                                        gain[:, g:g + 1], rstd[:, h * HALF:(h + 1) * HALF],
                                        ALU.mult, ALU.mult).then_inc(S["nt"], 1)

            def keep_lo(ph, u, j, h):
                c = slice(h * HALF, (h + 1) * HALF)
                ve.wait_ge(S["nh"], at(ph, "nh", u + 1))
                ve.tensor_tensor(hT[:, 1, j, c], psD[2 + u % 2][:, :], hT[:, 0, j, c].bitcast(F32),
                                 ALU.subtract).then_inc(S["nl"], 1)

            def units(ph, n, u0, h, tiles, g):
                reciprocal(ph, n, h)
                for j in range(len(tiles) + 1):
                    if j < len(tiles):
                        if u0 + j >= 2:
                            ve.wait_ge(S["nl"], at(ph, "nl", u0 + j - 1))
                        scaled(ph, u0 + j, h, tiles[j][0], g + j)
                    if j >= 1:
                        keep_lo(ph, u0 + j - 1, tiles[j - 1][1], h)

            def norm(ph, g):
                ve.wait_ge(S["const"], 48)
                for h in range(2):
                    units(ph, h, KT * h, h, [(x3[:, j, :], j) for j in range(KT)], g)

            ve.wait_ge(S["xc"], at("load", "xc", 8))
            norm("norm_a0", 0)

            def attention(ph, it, nsc, nfix, window, bank0, table, ready, build):
                for t in range(NSTEP + 5):
                    if t < NSTEP:
                        e, i = t // QB, t % QB
                        _, nk, off = window(i)
                        if t % QB == 0:
                            ready(e, it)
                        ve.wait_ge(S["sc"], at(ph, "sc", nfix + t + 1, it, nsc))
                        if t >= 2:
                            ve.wait_ge(S["tp"], at(ph, "tp", 2 + 2 * (t - 2) + 2, it, 34))
                        plain(ve)
                        ve.tensor_tensor_reduce(score[t % 2][:, 0:nk], psS[(t + bank0) % 2][:, 0:nk],
                                                table(e)[:, off:off + nk], -1.0, BIG, ALU.add, ALU.min,
                                                mneg[:, t % 2:t % 2 + 1]).then_inc(S["red"], 1)
                    if 1 <= t <= NSTEP:
                        u = t - 1
                        nk = window(u % QB)[1]
                        ve.wait_ge(S["ex"], at(ph, "ex", u + 1, it, 16))
                        r = rden[:, u % 2:u % 2 + 1]
                        ve.reciprocal(r, den[:, u % 2:u % 2 + 1]).then_inc(S["rc"], 1)
                        ve.wait_ge(S["rc"], at(ph, "rc", u + 1, it, 16))
                        s = score[u % 2][:, 0:nk]
                        ve.tensor_scalar(s, s, r, None, ALU.mult).then_inc(S["nm"], 1)
                    if 2 <= t < NSTEP + 2:
                        u = t - 2
                        nt = window(u % QB)[1] // P
                        cut = (nt + 1) // 2
                        g, q = u // 2, (u % 2) * P
                        for b, (j0, j1) in enumerate(((0, cut), (cut, nt))):
                            ve.wait_ge(S["hi"], at(ph, "hi", 2 + 2 * u + b + 1, it, 34))
                            ve.tensor_tensor(PT[:, g % 2, 1, j0:j1, q:q + P],
                                             blocks(psD[b][:, 0:(j1 - j0) * P]),
                                             PT[:, g % 2, 0, j0:j1, q:q + P].bitcast(F32),
                                             ALU.subtract).then_inc(S["lo"], 1)
                    if t == 3 and build:
                        build(1, it)
                    if t >= 5 and t % 2 == 1:
                        g = (t - 5) // 2
                        if g < QB:
                            ve.wait_ge(S["oc"], at(ph, "oc", g + 1, it, 8))
                            ve.wait_ge(S[f"od{g % 2}"], at(ph, f"od{g % 2}", g // 2, it, 4))
                            ve.tensor_tensor(o_out[:, g % 2, :], psD[2 + g % 2][0:HD, 0:256],
                                             o_lo[:, g % 2, :], ALU.add).then_inc(S["oa"], 1)

            def keep_v(ph, it):
                for b in range(2):
                    ve.wait_ge(S["hi"], at(ph, "hi", b + 1, it, 34))
                    v = vv[:, 4 * b:4 * b + 4, :, :]
                    ve.tensor_tensor(v[:, :, :, HD:P], psD[b][:, :].rearrange("p (k e d) -> p k e d", k=4, e=2),
                                     v[:, :, :, 0:HD].bitcast(F32), ALU.subtract).then_inc(S["lo"], 1)

            def even_phase(ph, window, table, ready, build):
                with ve.Fori(0, 4, 1) as it:
                    if build:
                        build(0, it)
                    for e in range(2):
                        kh = qk[:, 3 * e + 1, :].bitcast(F32)
                        for d in range(2):
                            ve.wait_ge(S["kq_hi"], at(ph, "kq_hi", 2 * e + 2, it, 6))
                            ve.tensor_tensor(qk[d * HD:(d + 1) * HD, 3 * e + 2, :],
                                             psS[0][e * HD:(e + 1) * HD, :], kh[0:HD, :],
                                             ALU.subtract).then_inc(S["kq_lo"], 1)
                    for e in range(2):
                        ve.wait_ge(S["kq_hi"], at(ph, "kq_hi", 5 + e, it, 6))
                        ve.scalar_tensor_tensor(flipped(qk[HD:P, 3 * e, :]),
                                                blocks(psS[1][e * HD:(e + 1) * HD, :]), HD ** -0.5,
                                                flipped(qk[0:HD, 3 * e, :]).bitcast(F32),
                                                ALU.mult, ALU.subtract).then_inc(S["kq_lo"], 1)
                    keep_v(ph, it)
                    attention(ph, it, 19, 3, window, 1, table, ready, build)

            def rel_table(e):
                return xT[:, TB_A + e * TW:TB_A + (e + 1) * TW]

            def off_table(e):
                return xT[:, TB_B + e * 2 * NROW * GRID:TB_B + (e + 1) * 2 * NROW * GRID]

            def build_b(e, it):
                if e == 0:
                    ve.wait_ge(S["bm"], at("attn_b", "bm", 1))
                ve.wait_ge(S["of"], at("attn_b", "of", 2 * e + 2, it, 4))
                rows = "p (r c) -> p r c"
                off = xT[:, OFF_B:OFF_B + NROW * GRID]
                col = xT[:, MASK_B:MASK_B + GRID].unsqueeze(1).broadcast_to([P, NROW, GRID])
                ve.tensor_tensor(off_table(e)[:, 0:NROW * GRID].rearrange(rows, c=GRID),
                                 off.rearrange(rows, c=GRID), col, ALU.add).then_inc(S["bb"], 1)
                ve.tensor_tensor(off_table(e)[:, NROW * GRID:2 * NROW * GRID], off,
                                 xT[:, MASK_B + GRID:MASK_B + (NROW + 1) * GRID], ALU.add)\
                    .then_inc(S["bb"], 1)

            even_phase("attn_a", a_window, rel_table,
                       lambda e, it: ve.wait_ge(S[f"tb{e}"], at("attn_a", f"tb{e}", 1, it, 1)), None)
            even_phase("attn_b", b_window, off_table,
                       lambda e, it: ve.wait_ge(S["bb"], at("attn_b", "bb", 2 * e + 2, it, 4)), build_b)

            def proj(ph):
                for j in range(KT):
                    ve.wait_ge(S["nh"], at(ph, "nh", j + 1))
                    ve.tensor_tensor(hT[:, 1, j, :], x3[:, j, :], hT[:, 0, j, :].bitcast(F32),
                                     ALU.subtract).then_inc(S["nl"], 1)
                for b in range(2):
                    ve.wait_ge(S[f"xr{b}"], at(ph, f"xr{b}", 1))
                with ve.Fori(0, 4, 1) as it:
                    for n in range(2):
                        ve.wait_ge(S["sc"], at(ph, "sc", n + 1, it, 2))
                        xm = xT[:, bass.ds(it * (2 * SEQ) + n * SEQ, SEQ)]
                        ve.tensor_tensor(xm, psS[n][:, :], xm, ALU.add).then_inc(S["xa"], 1)

            def ffn(ph):
                with ve.Fori(0, NFF, 1) as it:
                    for f in range(2):
                        for h in range(2):
                            c = slice(h * HALF, (h + 1) * HALF)
                            n = 2 * f + h + 1
                            ve.wait_ge(S["sl"], at(ph, "sl", n, it, 4))
                            ve.wait_ge(S["sc"], at(ph, "sc", 4 * f + 2 + h + 1, it, 8))
                            ve.tensor_tensor(row[:, c], psS[1][:, c], row[:, c], ALU.mult)\
                                .then_inc(S["pr"], 1)
                            ve.wait_ge(S["ah"], at(ph, "ah", n, it, 4))
                            ve.tensor_tensor(act[:, f, 1, c], row[:, c], act[:, f, 0, c].bitcast(F32),
                                             ALU.subtract).then_inc(S["al"], 1)
                    for h in range(2):
                        for m in range(KT):
                            n = h * KT + m
                            ve.wait_ge(S["dn"], at(ph, "dn", n + 1, it, 16))
                            xm = x3[:, m, h * HALF:(h + 1) * HALF]
                            ve.tensor_tensor(xm, psD[n % 4][:, :], xm, ALU.add).then_inc(S["xa"], 1)
                    ve.wait_ge(S["xa"], at(ph, "xa", 16, it, 16))

            proj("proj_0")
            ve.wait_ge(S["xa"], at("norm_f0", "xa", 0))
            norm("norm_f0", 16)
            ffn("ffn_0")
            norm("norm_a1", 8)
            units("latent", 0, 0, 0, [(x3[:, j, :], j) for j in range(QT)], 40)
            units("latent", 1, QT, 1, [(x3[:, j, :], j) for j in range(QT)], 40)
            units("latent", 2, 2 * QT, 0, [(x3[:, QT, :], QT)], 43)
            units("latent", 3, 2 * QT + 1, 1, [(x3[:, QT, :], QT)], 43)
            swap = [(i + ROPE // 2) % ROPE for i in range(ROPE)]

            def rotate(ph, it, per, src, n):
                plain(ve)
                ve.stream_shuffle(row[0:n, :], src, swap).then_inc(S["rp"], 1)
                ve.tensor_tensor(psS[1][0:n, :], src, xT[0:n, COS:COS + SEQ], ALU.mult).then_inc(S["rp"], 1)
                ve.wait_ge(S["rp"], at(ph, "rp", 2, it, per))
                ve.tensor_tensor(row[0:n, :], row[0:n, :], xT[0:n, SIN:SIN + SEQ], ALU.mult)\
                    .then_inc(S["rp"], 1)
                ve.wait_ge(S["rp"], at(ph, "rp", 3, it, per))
                ve.tensor_tensor(psS[1][0:n, :], psS[1][0:n, :], row[0:n, :], ALU.add).then_inc(S["rp"], 1)

            ve.wait_ge(S["cs"], at("latent", "cs", 2))
            ve.wait_ge(S["raw"], at("latent", "raw", 5))
            rotate("latent", 0, 0, x3[0:ROPE, 4, :], ROPE)
            for e in range(2):
                ve.wait_ge(S["kr_hi"], at("latent", "kr_hi", 2))
                kh, kl = latent_ops(e)[2:]
                ve.tensor_tensor(kl[HD:UQ, :], psS[1][0:ROPE, :], kh[HD:UQ, :].bitcast(F32), ALU.subtract)\
                    .then_inc(S["kr_lo"], 1)
            with ve.Fori(0, NC_PAIRS, 1) as it:
                ph = "attn_c"
                for e in range(2):
                    ve.wait_ge(S["kq_hi"], at(ph, "kq_hi", 1 + e, it, 6))
                    kh, kl = latent_ops(e)[2:]
                    ve.tensor_tensor(kl[0:HD, :], psS[0][e * HD:(e + 1) * HD, :], kh[0:HD, :].bitcast(F32),
                                     ALU.subtract).then_inc(S["kq_lo"], 1)
                for e in range(2):
                    ve.wait_ge(S["kq_hi"], at(ph, "kq_hi", 3 + e, it, 6))
                    qh, ql = latent_ops(e)[:2]
                    ve.scalar_tensor_tensor(flipped(ql[0:HD, :]), blocks(psS[1][e * HD:(e + 1) * HD, :]),
                                            C_SCALE, flipped(qh[0:HD, :]).bitcast(F32),
                                            ALU.mult, ALU.subtract).then_inc(S["kq_lo"], 1)
                keep_v(ph, it)
                ve.wait_ge(S["ra"], at(ph, "ra", 1, it, 1))
                rotate(ph, it, 4, rstd[0:HD, :], HD)
                for e in range(2):
                    ve.wait_ge(S["kq_hi"], at(ph, "kq_hi", 5 + e, it, 6))
                    qh, ql = latent_ops(e)[:2]
                    ve.tensor_tensor(flipped(ql[HD:UQ, :]), blocks(psS[1][e * ROPE:(e + 1) * ROPE, :]),
                                     flipped(qh[HD:UQ, :]).bitcast(F32), ALU.subtract)\
                        .then_inc(S["kq_lo"], 1)
                attention(ph, it, 20, 4, a_window, 0, rel_table,
                          lambda e, it: ve.wait_ge(S[f"tb{e}"], at("attn_c", f"tb{e}", 1, it, 1)), None)
            proj("proj_1")
            ve.wait_ge(S["xa"], at("norm_f1", "xa", 0))
            norm("norm_f1", 24)
            ffn("ffn_1")
            for h in range(2):
                reciprocal("last", h, h)
                for j in range(KT):
                    xm = x3[:, j, h * HALF:(h + 1) * HALF]
                    ve.scalar_tensor_tensor(xm, xm, gain[:, 32 + j:33 + j], rstd[:, h * HALF:(h + 1) * HALF],
                                            ALU.mult, ALU.mult).then_inc(S["nt"], 1)
            for t in range(QB):
                ve.wait_ge(S["yt"], at("last", "yt", t + 1))
                if t == 0:
                    ve.wait_ge(S["ws"], at("last", "ws", 0))
                if t >= 2:
                    ve.wait_ge(S[f"yo{t % 2}"], at("last", f"yo{t % 2}", t // 2))
                ve.tensor_copy(stage[:, t % 2, :], psS[t % 2][:, :]).then_inc(S["yc"], 1)


def shape_tables(np):
    eye = np.eye(P, dtype=np.float32)
    rel = np.arange(REL) - (SEQ - 1)
    n = np.abs(rel)
    large = 8 + (np.log(np.maximum(n, 8) / 8.0) / np.log(128.0) * 8).astype(np.int64)
    bucket = np.where(rel > 0, 16, 0) + np.where(n < 8, n, np.minimum(large, 15))
    onehot = np.zeros((33, REL), np.float32)
    onehot[bucket, np.arange(REL)] = 1.0
    seen = (n <= 64) * 1 + ((n <= 256) & (n % 4 == 0)) + ((n <= SEQ) & (n % 16 == 0))
    onehot[32] = np.where(seen > 0, np.log(np.maximum(seen, 1)), -1e30)
    freqs = np.float32(10000.0) ** (-np.arange(0, ROPE, 2, dtype=np.float32) / np.float32(ROPE))
    ang = (np.arange(SEQ, dtype=np.float32)[None, :] * freqs.astype(np.float32)[:, None]).astype(np.float32)
    cos = np.tile(np.cos(ang), (P // 16, 1)).astype(np.float32)
    sin = np.tile(np.concatenate([-np.sin(ang), np.sin(ang)]), (P // ROPE, 1)).astype(np.float32)
    mask = np.zeros((P, NROW + 1, GRID), np.float32)
    for p in range(P):
        dr, qc = 1 - p // GRID, GRID - 1 - p % GRID
        c0 = min(max(qc - 8, 0), GRID - 16)
        col = np.full(GRID, -1e30, np.float32)
        col[c0:c0 + 16] = 0.0
        mask[p, 0] = col
        for r in range(NROW):
            if -4 <= r - 6 - dr <= 3:
                mask[p, 1 + r] = col
            else:
                mask[p, 1 + r] = -1e30
    return {"eye": eye, "flip": np.ascontiguousarray(eye[::-1]), "onehot": onehot, "cos": cos, "sin": sin,
            "mask_b": mask.reshape(P, -1)}


def kernel(x, t5_table, attn_norm, ffn_norm, even_w_in, na_rpb, even_w_out, odd_w_in, mla_q_norm, mla_w_uq,
           mla_kv_norm, mla_w_uk, mla_w_uv, odd_w_out, ffn_w_gate, ffn_w_up, ffn_w_down, final_norm):
    import numpy as _np
    import concourse.bacc as _bacc
    from concourse import mybir as _mybir
    from concourse.bass_utils import run_bass_kernel_spmd as _run

    gains = _np.concatenate([_np.asarray(g).reshape(-1, P) for g in
                             (attn_norm, ffn_norm, final_norm, mla_q_norm, mla_kv_norm)]).T
    arrays = {"x": _np.asarray(x)[0], "t5": t5_table, "gains": gains, "w_even": _np.asarray(even_w_in)[0],
              "rpb": _np.asarray(na_rpb).reshape(120, 31), "w_even_out": _np.asarray(even_w_out)[0],
              "w_odd": _np.asarray(odd_w_in)[0], "w_uq": _np.asarray(mla_w_uq)[0],
              "w_uk": _np.asarray(mla_w_uk)[0], "w_uv": _np.asarray(mla_w_uv)[0],
              "w_odd_out": _np.asarray(odd_w_out)[0], "w_gate": ffn_w_gate, "w_up": ffn_w_up,
              "w_down": ffn_w_down, **shape_tables(_np)}
    nc = _bacc.Bacc("TRN2", target_bir_lowering=False, num_devices=1)
    ins, args = {}, []
    for name, a in arrays.items():
        a = _np.ascontiguousarray(a)
        ins[f"in_{name}"] = a
        args.append(nc.dram_tensor(f"in_{name}", a.shape, _mybir.dt.from_np(a.dtype), kind="ExternalInput").ap())
    args.append(nc.dram_tensor("out_0", (SEQ, DM), F32, kind="ExternalOutput").ap())
    build(nc, *args)
    r = _run(nc, [ins], core_ids=[0])
    return r.results[0]["out_0"].reshape(1, SEQ, DM)
```
